# Optimizing a Trainium2 kernel written in Bass

```python
import jax, jax.numpy as jnp
from jax import lax
import numpy as np

D_MODEL = 2048
BATCH = 1
SEQ = 256
DEPTH = 2

CHUNK = 64
N_MIXERS = 2
N_A = (DEPTH + N_MIXERS - 1) // N_MIXERS
N_B = DEPTH // N_MIXERS
NORM_EPS = 1e-6

SGU_BLOCK = 128
SGU_WIDTH = 2 * D_MODEL
SGU_GROUPS = 16
SGU_GROUP_DIM = SGU_WIDTH // SGU_GROUPS

MLA_HEADS = 16
Q_LORA_RANK = 448
KV_LORA_RANK = 512
QK_NOPE_DIM = 128
QK_ROPE_DIM = 64
V_HEAD_DIM = 128
MLA_WIDTH = MLA_HEADS * V_HEAD_DIM
ROPE_THETA = 10000.0
Q_BLOCK = 128


def rms_norm(x, g):
    xf = x.astype(jnp.float32)
    y = xf * lax.rsqrt(jnp.mean(xf * xf, axis=-1, keepdims=True) + NORM_EPS)
    return (y * g.astype(jnp.float32)).astype(x.dtype)

def layer_norm(x, g):
    xf = x.astype(jnp.float32)
    mu = jnp.mean(xf, axis=-1, keepdims=True)
    var = jnp.mean(jnp.square(xf - mu), axis=-1, keepdims=True)
    return ((xf - mu) * lax.rsqrt(var + NORM_EPS) * g.astype(jnp.float32)).astype(x.dtype)

def apply_rope(x, cos, sin):
    xf = x.astype(jnp.float32)
    x1, x2 = jnp.split(xf, 2, axis=-1)
    return jnp.concatenate([x1 * cos - x2 * sin, x1 * sin + x2 * cos], axis=-1).astype(x.dtype)

def sgu_mixer(h, w_in, norm_g, w_s, b_s, w_out):
    B, S, _ = h.shape
    u, v, z = jnp.split(h @ w_in, 3, axis=-1)
    u = jax.nn.gelu(u, approximate=False)
    v = layer_norm(jax.nn.gelu(v, approximate=False), norm_g)
    t_chunk = jnp.arange(SGU_BLOCK) // CHUNK
    mask = (t_chunk[None, :] <= t_chunk[:, None]).astype(w_s.dtype)
    w = w_s * mask[None]
    vb = v.reshape(B, S // SGU_BLOCK, SGU_BLOCK, SGU_GROUPS, SGU_GROUP_DIM)
    vm = jnp.einsum('gts,bnsgc->bntgc', w, vb) + b_s.T[:, :, None]
    y = u * vm.reshape(B, S, SGU_WIDTH) * jax.nn.silu(z)
    return y @ w_out

def chunk_causal_attention(q_nope, q_rope, k_nope, k_rope, v):
    B, S, H, _ = q_nope.shape
    nqb = S // Q_BLOCK
    scale = (QK_NOPE_DIM + QK_ROPE_DIM) ** -0.5
    k_chunk = jnp.arange(S) // CHUNK

    def to_blocks(t):
        return jnp.moveaxis(t.reshape(B, nqb, Q_BLOCK, *t.shape[2:]), 1, 0)

    def one_block(args):
        idx, qn, qr = args
        s = (jnp.einsum('bqhd,bkhd->bhqk', qn, k_nope)
             + jnp.einsum('bqhd,bkd->bhqk', qr, k_rope)).astype(jnp.float32) * scale
        q_chunk = (idx * Q_BLOCK + jnp.arange(Q_BLOCK)) // CHUNK
        mask = k_chunk[None, :] <= q_chunk[:, None]
        p = jax.nn.softmax(jnp.where(mask, s, -1e30), axis=-1).astype(v.dtype)
        return jnp.einsum('bhqk,bkhd->bqhd', p, v)

    out = lax.map(one_block, (jnp.arange(nqb), to_blocks(q_nope), to_blocks(q_rope)))
    return jnp.moveaxis(out, 0, 1).reshape(B, S, H, V_HEAD_DIM)

def mla_mixer(h, w_in, q_norm_g, kv_norm_g, w_uq, w_ukv, w_out):
    B, S, _ = h.shape
    o1 = Q_LORA_RANK
    o2 = o1 + KV_LORA_RANK
    o3 = o2 + QK_ROPE_DIM
    cq, ckv, k_rope, z = jnp.split(h @ w_in, [o1, o2, o3], axis=-1)
    q = (rms_norm(cq, q_norm_g) @ w_uq).reshape(B, S, MLA_HEADS, QK_NOPE_DIM + QK_ROPE_DIM)
    kv = (rms_norm(ckv, kv_norm_g) @ w_ukv).reshape(B, S, MLA_HEADS, QK_NOPE_DIM + V_HEAD_DIM)
    q_nope, q_rope = q[..., :QK_NOPE_DIM], q[..., QK_NOPE_DIM:]
    k_nope, v = kv[..., :QK_NOPE_DIM], kv[..., QK_NOPE_DIM:]
    pos = jnp.arange(S, dtype=jnp.float32)
    inv_freq = ROPE_THETA ** (-jnp.arange(0, QK_ROPE_DIM, 2, dtype=jnp.float32) / QK_ROPE_DIM)
    ang = pos[:, None] * inv_freq[None, :]
    cos, sin = jnp.cos(ang), jnp.sin(ang)
    q_rope = apply_rope(q_rope, cos[:, None, :], sin[:, None, :])
    k_rope = apply_rope(k_rope, cos, sin)
    o = chunk_causal_attention(q_nope, q_rope, k_nope, k_rope, v)
    y = o.reshape(B, S, MLA_WIDTH) * jax.nn.silu(z)
    return y @ w_out

def first_inputs(seed: int = 0) -> dict:
    key = jax.random.key(seed)
    ks = jax.random.split(key, 17)
    f32 = jnp.float32
    D = D_MODEL

    def nrm(k, shape, s):
        return jax.random.normal(k, shape, f32) * s

    def gain(k, shape):
        return 1.0 + 0.05 * jax.random.normal(k, shape, f32)

    mla_in_cols = Q_LORA_RANK + KV_LORA_RANK + QK_ROPE_DIM + MLA_WIDTH
    return {
        'x': nrm(ks[0], (BATCH, SEQ, D), 1.0),
        'c': nrm(ks[1], (BATCH, D), 1.0),
        'ada_w': nrm(ks[2], (DEPTH, D, 3 * D), 0.5 * D ** -0.5),
        'ada_b': nrm(ks[3], (DEPTH, 3 * D), 0.01),
        'pre_g': gain(ks[4], (DEPTH, D)),
        'post_g': gain(ks[5], (DEPTH, D)),
        'sgu_w_in': nrm(ks[6], (N_A, D, 3 * SGU_WIDTH), D ** -0.5),
        'sgu_norm_g': gain(ks[7], (N_A, SGU_WIDTH)),
        'sgu_w_s': nrm(ks[8], (N_A, SGU_GROUPS, SGU_BLOCK, SGU_BLOCK), SGU_BLOCK ** -0.5),
        'sgu_b_s': gain(ks[9], (N_A, SGU_GROUPS, SGU_BLOCK)),
        'sgu_w_out': nrm(ks[10], (N_A, SGU_WIDTH, D), SGU_WIDTH ** -0.5),
        'mla_w_in': nrm(ks[11], (N_B, D, mla_in_cols), D ** -0.5),
        'mla_q_norm_g': gain(ks[12], (N_B, Q_LORA_RANK)),
        'mla_kv_norm_g': gain(ks[13], (N_B, KV_LORA_RANK)),
        'mla_w_uq': nrm(ks[14], (N_B, Q_LORA_RANK, MLA_HEADS * (QK_NOPE_DIM + QK_ROPE_DIM)), Q_LORA_RANK ** -0.5),
        'mla_w_ukv': nrm(ks[15], (N_B, KV_LORA_RANK, MLA_HEADS * (QK_NOPE_DIM + V_HEAD_DIM)), KV_LORA_RANK ** -0.5),
        'mla_w_out': nrm(ks[16], (N_B, MLA_WIDTH, D), MLA_WIDTH ** -0.5),
    }

def first_block(x, c, ada_w, ada_b, pre_g, post_g, sgu_w_in, sgu_norm_g, sgu_w_s, sgu_b_s, sgu_w_out,
              mla_w_in, mla_q_norm_g, mla_kv_norm_g, mla_w_uq, mla_w_ukv, mla_w_out):
    cond = jax.nn.silu(c)
    for i in range(DEPTH):
        mod = cond @ ada_w[i] + ada_b[i]
        shift, scale, gate = jnp.split(mod, 3, axis=-1)
        h = rms_norm(x, pre_g[i]) * (1 + scale[:, None, :]) + shift[:, None, :]
        j = i // N_MIXERS
        if i % N_MIXERS == 0:
            y = sgu_mixer(h, sgu_w_in[j], sgu_norm_g[j], sgu_w_s[j], sgu_b_s[j], sgu_w_out[j])
        else:
            y = mla_mixer(h, mla_w_in[j], mla_q_norm_g[j], mla_kv_norm_g[j], mla_w_uq[j], mla_w_ukv[j], mla_w_out[j])
        x = x + gate[:, None, :] * rms_norm(y, post_g[i])
    return x


DEPTH_2 = 1

HG_HEADS = 8
HG_KDIM = 128
HG_VDIM = 128
HG_QF = HG_HEADS * HG_KDIM
HG_WIDTH = HG_HEADS * HG_VDIM
HG_CHUNK = 64
AT_HEADS = 16
AT_KV_HEADS = 2
AT_HEAD_DIM = 64
AT_GROUP = AT_HEADS // AT_KV_HEADS
AT_WIDTH = AT_HEADS * AT_HEAD_DIM
AT_KV_WIDTH = AT_KV_HEADS * AT_HEAD_DIM
WINDOW = 128
BLOCK = 128
D_FF = 4 * D_MODEL
EPS = 1e-6

SPLIT_SIZES = (HG_QF, HG_QF, HG_WIDTH, HG_WIDTH, AT_WIDTH, AT_KV_WIDTH, AT_KV_WIDTH, D_MODEL, D_MODEL)
D_IN = sum(SPLIT_SIZES)


def rmsnorm(x, g):
    xf = x.astype(jnp.float32)
    y = xf * lax.rsqrt(jnp.mean(xf * xf, axis=-1, keepdims=True) + EPS)
    return (y * g.astype(jnp.float32)).astype(x.dtype)

def alibi_slopes(n):
    return jnp.asarray(2.0 ** (-8.0 * (np.arange(n, dtype=np.float32) + 1.0) / n), dtype=jnp.float32)

def hgrn2(q, f_logit, i, lb):
    bsz, t_len, _ = q.shape
    n_chunks = t_len // HG_CHUNK
    c = HG_CHUNK
    lb = lb.astype(jnp.float32)
    qf = jax.nn.silu(q.astype(jnp.float32))
    fg = lb + (1.0 - lb) * jax.nn.sigmoid(f_logit.astype(jnp.float32))
    kf = 1.0 - fg
    logf = jnp.log(fg)

    def chunks(a, d):
        return a.reshape(bsz, n_chunks, c, HG_HEADS, d).transpose(0, 1, 3, 2, 4)

    q_c = chunks(qf, HG_KDIM)
    k_c = chunks(kf, HG_KDIM)
    g_c = chunks(logf, HG_KDIM)
    v_c = chunks(i.astype(jnp.float32), HG_VDIM)
    cum = jnp.cumsum(g_c, axis=3)
    ref = cum[:, :, :, c // 2 - 1:c // 2]
    a = jnp.einsum('bnhck,bnhsk->bnhcs', q_c * jnp.exp(cum - ref), k_c * jnp.exp(ref - cum))
    causal = jnp.tril(jnp.ones((c, c), dtype=bool))
    a = jnp.where(causal, a, 0.0)
    o_intra = jnp.einsum('bnhcs,bnhsv->bnhcv', a, v_c)
    last = cum[:, :, :, -1:]
    q_out = q_c * jnp.exp(cum)
    k_state = k_c * jnp.exp(last - cum)
    decay_last = jnp.exp(last[:, :, :, 0, :])

    def step(state, xs):
        qo, ks, vs, dl = xs
        o = jnp.einsum('bhck,bhkv->bhcv', qo, state)
        state = dl[..., None] * state + jnp.einsum('bhck,bhcv->bhkv', ks, vs)
        return state, o

    xs = (jnp.moveaxis(q_out, 1, 0), jnp.moveaxis(k_state, 1, 0),
          jnp.moveaxis(v_c, 1, 0), jnp.moveaxis(decay_last, 1, 0))
    s0 = jnp.zeros((bsz, HG_HEADS, HG_KDIM, HG_VDIM), jnp.float32)
    _, o_inter = lax.scan(step, s0, xs)
    o = o_intra + jnp.moveaxis(o_inter, 0, 1)
    return o.transpose(0, 1, 3, 2, 4).reshape(bsz, t_len, HG_HEADS, HG_VDIM)

def swa_sinks(q, k, v, sinks):
    bsz, t_len = q.shape[0], q.shape[1]
    nb = t_len // BLOCK
    qb = q.reshape(bsz, nb, BLOCK, AT_KV_HEADS, AT_GROUP, AT_HEAD_DIM)
    pad = jnp.zeros((bsz, BLOCK, AT_KV_HEADS, AT_HEAD_DIM), k.dtype)

    def band(a):
        ap = jnp.concatenate([pad, a], axis=1).reshape(bsz, nb + 1, BLOCK, AT_KV_HEADS, AT_HEAD_DIM)
        return jnp.concatenate([ap[:, :-1], ap[:, 1:]], axis=2)

    kb = band(k)
    vb = band(v)
    scale = AT_HEAD_DIM ** -0.5
    s = jnp.einsum('bnqhgd,bnkhd->bnhgqk', qb, kb).astype(jnp.float32) * scale
    qi = jnp.arange(BLOCK)[:, None]
    kj = jnp.arange(2 * BLOCK)[None, :]
    dist = qi + BLOCK - kj
    in_band = (dist >= 0) & (dist < WINDOW)
    blk = jnp.arange(nb)[:, None, None]
    valid = in_band[None] & ((blk > 0) | (kj[None] >= BLOCK))
    slopes = alibi_slopes(AT_HEADS)
    bias = -slopes[:, None, None] * dist.astype(jnp.float32)[None]
    s = s + bias.reshape(AT_KV_HEADS, AT_GROUP, BLOCK, 2 * BLOCK)[None, None]
    s = jnp.where(valid[None, :, None, None], s, -jnp.inf)
    sink = sinks.astype(jnp.float32).reshape(AT_KV_HEADS, AT_GROUP)[None, None, :, :, None, None]
    m = jnp.maximum(jnp.max(s, axis=-1, keepdims=True), sink)
    p = jnp.exp(s - m)
    p = p / (jnp.sum(p, axis=-1, keepdims=True) + jnp.exp(sink - m))
    o = jnp.einsum('bnhgqk,bnkhd->bnqhgd', p.astype(v.dtype), vb)
    return o.reshape(bsz, t_len, AT_WIDTH)

def second_inputs(seed: int = 0) -> dict:
    key = jax.random.key(seed)
    ks = jax.random.split(key, 14)
    f32 = jnp.float32
    L = DEPTH_2
    return {
        "x": jax.random.normal(ks[0], (BATCH, SEQ, D_MODEL), f32),
        "norm_mix": 1.0 + 0.1 * jax.random.normal(ks[1], (L, D_MODEL), f32),
        "w_in": jax.random.normal(ks[2], (L, D_MODEL, D_IN), f32) * D_MODEL ** -0.5,
        "lb_logits": 0.5 * jax.random.normal(ks[3], (L, HG_QF), f32),
        "hg_norm": 1.0 + 0.1 * jax.random.normal(ks[4], (L, HG_VDIM), f32),
        "q_norm": 1.0 + 0.1 * jax.random.normal(ks[5], (L, AT_HEAD_DIM), f32),
        "k_norm": 1.0 + 0.1 * jax.random.normal(ks[6], (L, AT_HEAD_DIM), f32),
        "sinks": 0.5 * jax.random.normal(ks[7], (L, AT_HEADS), f32),
        "w_hg_out": jax.random.normal(ks[8], (L, HG_WIDTH, D_MODEL), f32) * HG_WIDTH ** -0.5,
        "w_at_out": jax.random.normal(ks[9], (L, AT_WIDTH, D_MODEL), f32) * AT_WIDTH ** -0.5,
        "w_out": jax.random.normal(ks[10], (L, D_MODEL, D_MODEL), f32) * D_MODEL ** -0.5,
        "norm_ffn": 1.0 + 0.1 * jax.random.normal(ks[11], (L, D_MODEL), f32),
        "w_up": jax.random.normal(ks[12], (L, D_MODEL, D_FF), f32) * D_MODEL ** -0.5,
        "w_down": jax.random.normal(ks[13], (L, D_FF, D_MODEL), f32) * (0.5 * D_FF ** -0.5),
    }

def second_block(x, norm_mix, w_in, lb_logits, hg_norm, q_norm, k_norm, sinks,
              w_hg_out, w_at_out, w_out, norm_ffn, w_up, w_down):
    bsz, t_len, _ = x.shape
    lbp = jax.nn.softmax(lb_logits.astype(jnp.float32), axis=0)
    lower_bounds = jnp.cumsum(lbp, axis=0) - lbp[0:1]
    offsets = [int(v) for v in np.cumsum(SPLIT_SIZES)[:-1]]
    for l in range(DEPTH_2):
        h = rmsnorm(x, norm_mix[l])
        z = h @ w_in[l]
        hq, hf, hi, hgate, aq, ak, av, g_hg, g_at = jnp.split(z, offsets, axis=-1)
        o_hg = hgrn2(hq, hf, hi, lower_bounds[l]).astype(x.dtype)
        o_hg = rmsnorm(o_hg, hg_norm[l]) * jax.nn.silu(hgate.reshape(bsz, t_len, HG_HEADS, HG_VDIM))
        y_hg = o_hg.reshape(bsz, t_len, HG_WIDTH) @ w_hg_out[l]
        qa = rmsnorm(aq.reshape(bsz, t_len, AT_HEADS, AT_HEAD_DIM), q_norm[l])
        ka = rmsnorm(ak.reshape(bsz, t_len, AT_KV_HEADS, AT_HEAD_DIM), k_norm[l])
        va = av.reshape(bsz, t_len, AT_KV_HEADS, AT_HEAD_DIM)
        y_at = swa_sinks(qa, ka, va, sinks[l]) @ w_at_out[l]
        mixed = jax.nn.sigmoid(g_hg) * y_hg + jax.nn.sigmoid(g_at) * y_at
        x = x + mixed @ w_out[l]
        h2 = rmsnorm(x, norm_ffn[l])
        x = x + jnp.square(jax.nn.relu(h2 @ w_up[l])) @ w_down[l]
    return x


def setup_inputs(seed=0):
    out = dict(first_inputs(seed))
    for name, value in second_inputs(seed + 1).items():
        if name != "x":
            out[name + "_2"] = value
    return out


def reference(
    x, c, ada_w, ada_b, pre_g, post_g, sgu_w_in, sgu_norm_g, sgu_w_s, sgu_b_s, sgu_w_out,
    mla_w_in, mla_q_norm_g, mla_kv_norm_g, mla_w_uq, mla_w_ukv, mla_w_out, norm_mix_2, w_in_2,
    lb_logits_2, hg_norm_2, q_norm_2, k_norm_2, sinks_2, w_hg_out_2, w_at_out_2, w_out_2,
    norm_ffn_2, w_up_2, w_down_2,
):
    x = first_block(
        x, c, ada_w, ada_b, pre_g, post_g, sgu_w_in, sgu_norm_g, sgu_w_s, sgu_b_s, sgu_w_out,
        mla_w_in, mla_q_norm_g, mla_kv_norm_g, mla_w_uq, mla_w_ukv, mla_w_out,
    )
    return second_block(
        x, norm_mix_2, w_in_2, lb_logits_2, hg_norm_2, q_norm_2, k_norm_2, sinks_2, w_hg_out_2,
        w_at_out_2, w_out_2, norm_ffn_2, w_up_2, w_down_2,
    )


_drawn_inputs = setup_inputs


def setup_inputs(seed=0):
    import zlib

    import numpy as np

    out = dict(_drawn_inputs(seed))
    spreads = {}
    factors = {'ada_b': 2.765,
     'sgu_norm_g': 5.411,
     'sgu_b_s': 4.506,
     'mla_q_norm_g': 7.779,
     'mla_kv_norm_g': 3.465,
     'q_norm_2': 3.831,
     'k_norm_2': 5.216,
     'sinks_2': 27.317}
    for name, (base, spread) in spreads.items():
        noise = np.random.default_rng([zlib.crc32(name.encode()), seed]).standard_normal(out[name].shape)
        drawn = base * np.exp(spread * noise) if base else spread * noise
        out[name] = __import__('jax').numpy.asarray(drawn.astype(out[name].dtype))
    for name, factor in factors.items():
        out[name] = (out[name] * factor).astype(out[name].dtype)
    return out
```

```python
from contextlib import ExitStack, contextmanager

import concourse.bass as bass
import numpy as np
from concourse import mybir

ALU = mybir.AluOpType
ACT = mybir.ActivationFunctionType
F32 = mybir.dt.float32
F32R = mybir.dt.float32r
BF16 = mybir.dt.bfloat16
U32 = mybir.dt.uint32
AX = mybir.AxisListType.X

P = 128
T = 2
S = 256
D = 2048
KT = D // P
W2 = 4096
NB = 512
EPS = 1e-6
RAWS = 4
CHUNKS = 4
CW = 1024
AHEAD = 3
LAND = 64
MLA_SCALE = (128 + 64) ** -0.5
NEG = -1e30

C_ID, C_TRI, C_ROPE, C_MASK, C_DIST, C_SLOPE, C_END = 0, 128, 256, 512, 896, 1280, 1296
A_C, A_PRE, A_POST, A_MIX, A_FFN, A_KVG, A_ROWS = 0, 16, 48, 80, 96, 112, 116
B_ADA, B_BS, B_QG, B_ROWS = 0, 96, 112, 116


def constants():
    c = np.zeros((P, C_END), np.float32)
    i = np.arange(P)
    c[:, C_ID:C_ID + P] = np.eye(P)
    c[:, C_TRI:C_TRI + P] = (i[:, None] // 64 == i[None, :] // 64) & (i[:, None] <= i[None, :])
    freq = np.float32(10000.0) ** (-np.arange(0, 64, 2, dtype=np.float32) / np.float32(64))
    ang = freq[:, None] * np.arange(S, dtype=np.float32)[None, :]
    c[0:64, C_ROPE:C_ROPE + S] = np.concatenate([np.cos(ang)] * 2)
    c[64:128, C_ROPE:C_ROPE + S] = np.concatenate([-np.sin(ang), np.sin(ang)])
    late = (i[:, None] < 64) & (i[None, :] >= 64)
    c[:, C_MASK:C_MASK + P][late] = NEG
    c[:, C_MASK + 2 * P:C_MASK + 3 * P][late] = NEG
    here = (i[:, None] - i[None, :]).astype(np.float32)
    far = np.float32(1e33)
    c[:, C_DIST:C_DIST + P] = np.where(here >= 0, here, far)
    c[:, C_DIST + P:C_DIST + 2 * P] = np.where(here < 0, here + P, far)
    c[:, C_DIST + 2 * P:C_DIST + 3 * P] = np.where(here >= 0, here, far)
    c[:, C_SLOPE:C_SLOPE + 16] = -(2.0 ** (-8.0 * (np.arange(16, dtype=np.float32) + 1.0) / 16))
    return c


class Count:

    def __init__(self, base=0):
        self.base, self.each, self.turn = base, 0, None

    def at(self, more=0):
        v = self.base + more
        return v if self.turn is None else self.turn * self.each + v


class Counts:

    def __init__(self):
        self.by = {k: Count() for k in ("raw", "chunk", "acc", "stg", "tg", "ada", "nrm", "dv", "ac", "po", "head", "swa", "hg", "sq")}
        self.raw, self.chunk, self.acc, self.stg, self.tg, self.ada, self.nrm, self.dv, self.ac, self.po, self.head, self.swa, self.hg, self.sq = self.by.values()


@contextmanager
def turns(eng, n, n_turns, **each):
    start = {k: c.base for k, c in n.by.items()}
    with eng.Fori(0, n_turns) as i:
        for k, c in n.by.items():
            c.each, c.turn = each.get(k, 0), i
        yield i
    wrong = {k: c.base - start[k] for k, c in n.by.items() if c.base - start[k] != c.each and not (k == "raw" and c.base == start[k])}
    assert not wrong, wrong
    for k, c in n.by.items():
        c.turn, c.base = None, start[k] + n_turns * c.each


ADA_HEAD = 32
MIXED = 128


STAGED = 2 * 64


def raw_of(chunk):
    g = chunk // 2
    return ADA_HEAD + g + (g // 2 if g < MIXED else MIXED // 2)


def build(nc, d, out):
    ctx = ExitStack()
    with ctx:
        def sb(name, shape, dt=F32):
            return ctx.enter_context(nc.sbuf_tensor(name, shape, dt))

        def sem(name):
            return ctx.enter_context(nc.semaphore(name))

        x = sb("x", [P, T, D])
        a_hi, a_lo = sb("a_hi", [P, KT, S], F32R), sb("a_lo", [P, KT, S], F32R)
        v = sb("v", [P, T, W2])
        y = sb("y", [P, T, D])
        raw = sb("raw", [P, RAWS, 2 * CW])
        hi, lo = sb("hi", [P, CHUNKS, CW], F32R), sb("lo", [P, CHUNKS, CW], F32R)
        stage = sb("stage", [P, T, NB])
        tf = sb("tf", [P, 2, NB])
        acc = sb("acc", [P, NB])
        cst = sb("cst", [P, C_END])
        va, vb = sb("va", [P, A_ROWS]), sb("vb", [P, B_ROWS])
        mod = sb("mod", [P, 2, 48])
        cond = sb("cond", [P, KT])
        hscale = sb("hscale", [P, KT])
        gpost = sb("gpost", [P, KT])
        ones = sb("ones", [P, 1])
        ss, var, sd, rstd = (sb(k, [P, T]) for k in ("ss", "var", "sd", "rstd"))
        cnt = sb("cnt", [P, T, 8, 6])
        agg = sb("agg", [P, T, 2])
        with nc.sbuf_tensor("ws", [P, 16, P], F32) as ws, nc.sbuf_tensor("wt", [P, 16, P], F32) as wt:
            pass
        with ExitStack() as over:
            def ov(name, shape):
                return over.enter_context(nc.sbuf_tensor(name, shape, F32))
            qt_all = ov("qt_all", [P, 8, S])
            kt_all = ov("kt_all", [P, 2, S])
            v_at = ov("v_at", [P, T, P])
            rows = ov("rows", [P, 272])
            qt_cur = ov("qt_cur", [P, S])
            swa_s = ov("swa_s", [P, 384])
            swa_pt = ov("swa_pt", [P, 384])
            h_qf = ov("h_qf", [P, 2, T, P])
            h_k, h_g, h_v, h_gate = (ov(k, [P, T, P]) for k in ("h_k", "h_g", "h_v", "h_gate"))
            h_junk = over.enter_context(nc.sbuf_tensor("h_junk", [P, T, P], BF16))
            h_cum = ov("h_cum", [P, S])
            h_e = ov("h_e", [P, 4, S])
            h_a, h_kt = ov("h_a", [P, T, P]), ov("h_kt", [P, T, P])
            h_s = ov("h_s", [P, 3, P])
            nrm = ov("nrm", [P, 3, T, 18])
            w_nm, w_sum, w_es, w_rec = (ov(k, [P, T]) for k in ("w_nm", "w_sum", "w_es", "w_rec"))
            h_n = ov("h_n", [P, 3, T])
        b_hi, b_lo = sb("b_hi", [P, KT, S], F32R), sb("b_lo", [P, KT, S], F32R)

        h_q, h_f, kdup = h_qf[:, 0, :, :], h_qf[:, 1, :, :], h_qf
        oml, lb = tf[:, :, :].rearrange("p a b -> p (a b)"), stage[:, :, :].rearrange("p a b -> p (a b)")
        h_d = acc[:, :].rearrange("p (a b) -> p a b", a=2)
        junk = stage[:, :, :].rearrange("p t n -> p (t n)").bitcast(BF16)
        tick = sb("tick", [P, RAWS + 1])

        m_qn, m_kn, m_kr, m_qr, m_t = (y[:, 0, k * S:(k + 1) * S] for k in range(5))
        m_v = y[:, 0, 5 * S:6 * S].rearrange("p (t c) -> p t c", t=T)
        m_s, m_pt = y[:, 1, 0:384], y[:, 1, 384:768]
        m_max, m_sum, m_rec = y[:, 1, 768:770], y[:, 1, 770:772], y[:, 1, 772:774]
        m_t2 = y[:, 1, 1024:1024 + S]
        ident = cst[:, C_ID:C_ID + P]
        tri = cst[:, C_TRI:C_TRI + P]

        ps = ctx.enter_context(nc.psum_tensor("ps", [P, 8, NB], F32))

        landed = [sem(f"raw_landed{k}") for k in range(RAWS)]
        raw_free, hi_ready, lo_ready, chunk_used = (sem(k) for k in ("raw_free", "hi_ready", "lo_ready", "chunk_used"))
        acc_free, stage_free = sem("acc_free"), sem("stage_free")
        small_landed, x_landed, gain_landed, rows_landed = (sem(k) for k in ("small_landed", "x_landed", "gain_landed", "rows_landed"))
        set_up = sem("set_up")
        vec_turned, vec_kept, cond_ready = sem("vec_turned"), sem("vec_kept"), sem("cond_ready")
        ada_acc, ada_summed, ada_kept = sem("ada_acc"), sem("ada_summed"), sem("ada_kept")
        t_turned, t_kept, t_hi, t_lo = (sem(k) for k in ("t_turned", "t_kept", "t_hi", "t_lo"))
        n_ss, n_var, n_sd, n_rstd, n_out = (sem(k) for k in ("n_ss", "n_var", "n_sd", "n_rstd", "n_out"))
        v_ready, ln_done, sp_turned, sp_kept, sp_mixed, vm_act, vm_vec = (sem(k) for k in ("v_ready", "ln_done", "sp_turned", "sp_kept", "sp_mixed", "vm_act", "vm_vec"))
        gain_cols, gate_rows, x_updated = sem("gain_cols"), sem("gate_rows"), sem("x_updated")
        dv_step, ac_step, po_step = sem("dv_step"), sem("ac_step"), sem("po_step")
        c_ready, kr_ready, kr_kept = sem("c_ready"), sem("kr_ready"), sem("kr_kept")
        m_proj, m_evac, m_roped, m_scored, m_maxed, m_exped, m_turned, m_ptk, m_pv, m_rcp, m_out = (
            sem(k) for k in ("m_proj", "m_evac", "m_roped", "m_scored", "m_maxed", "m_exped", "m_turned", "m_ptk", "m_pv", "m_rcp", "m_out"))
        y_ready = sem("y_ready")
        q_cur, w_scored, w_maxed, w_exped, w_turned, w_ptk, w_pv, w_rcp, w_out = (
            sem(k) for k in ("q_cur", "w_scored", "w_maxed", "w_exped", "w_turned", "w_ptk", "w_pv", "w_rcp", "w_out"))
        h_in, h_fg, h_log, h_turned, h_cumk, h_diff, h_exp, h_prod, h_amm, h_am, h_ktk, h_upd, h_st, h_om, h_sq, h_v1, h_sd1, h_done = (
            sem(f"h_{k}") for k in ("in", "fg", "log", "turned", "cumk", "diff", "exp", "prod", "amm", "am", "ktk", "upd", "st", "om", "sq", "v1", "sd1", "done"))
        q_ss, q_sd, q_normed, q_turned, q_kept, q_rows = (sem(k) for k in ("q_ss", "q_sd", "q_normed", "q_turned", "q_kept", "q_rows"))
        stored = sem("stored")
        lb_diff, lb_exp, h_gn, h_kf = (sem(k) for k in ("lb_diff", "lb_exp", "h_gn", "h_kf"))
        wt_zero, h_a_zero = sem("wt_zero"), sem("h_a_zero")
        lb_ready = sem("lb_ready")

        block = ctx.enter_context(nc.Block())

        def kslab(w, r, col, width=NB, kts=4):
            return w.rearrange("(k p) n -> p k n", p=P)[:, kts * r:kts * (r + 1), bass.ds(col, width)]

        def load(sp, n, *parts):
            k = n.raw.base % RAWS
            sp.wait_ge(raw_free, n.raw.at(1))
            for place, source, adds in parts:
                sp.dma_start(place(raw[:, k, :]), source).then_inc(landed[k], adds)
            n.raw.base += 1

        def whole(kts=4, width=NB):
            return lambda s: s[:, 0:kts * width].rearrange("p (k n) -> p k n", k=kts)

        def sp_block(sp, n, w, col, k0=0, slabs=4, ada=None, half=0):
            for g in range(slabs):
                load(sp, n, (whole(), kslab(w, k0 + g, col), LAND))
                if ada is not None and g % 2:
                    load(sp, n, (whole(), kslab(ada[0], 2 * half + g // 2, ada[1]), LAND))

        def sp_pairs(sp, n, w, col, n_turns, k0=0, slabs=4, ada=None):
            per = 8 * slabs // 4 + (4 if ada is not None else 0)
            with turns(sp, n, n_turns, raw=per) as i:
                for b in range(2):
                    a = None if ada is None else (ada[0], i * NB + ada[1])
                    sp_block(sp, n, w, i * (2 * NB) + (col + b * NB), k0, slabs, a, b)

        @block.sync
        def _(sp):
            n = Counts()
            sp.wait_ge(set_up, 2)
            sp.dma_start(cst[:, :], d["constants"]).then_inc(small_landed, 16)
            ra, rb = tf[:, 0, 0:P], tf[:, 0, P:2 * P]
            small = [
                (ra[A_C:A_C + 16], d["c"].rearrange("a (r q) -> (a r) q", q=P)),
                (ra[A_PRE:A_PRE + 32], d["pre_g"].rearrange("a (r q) -> (a r) q", q=P)),
                (ra[A_POST:A_POST + 32], d["post_g"].rearrange("a (r q) -> (a r) q", q=P)),
                (ra[A_MIX:A_MIX + 16], d["norm_mix_2"].rearrange("a (r q) -> (a r) q", q=P)),
                (ra[A_FFN:A_FFN + 16], d["norm_ffn_2"].rearrange("a (r q) -> (a r) q", q=P)),
                (ra[A_KVG:A_KVG + 4], d["mla_kv_norm_g"].rearrange("a (r q) -> (a r) q", q=P)),
                (rb[B_ADA:B_ADA + 96], d["ada_b"].rearrange("a (r q) -> (a r) q", q=P)),
                (rb[B_BS:B_BS + 16], d["sgu_b_s"].rearrange("a g t -> (a g) t")),
                (rb[B_QG:B_QG + 4, 0:112], d["mla_q_norm_g"].rearrange("a (r q) -> (a r) q", q=112)),
            ]
            for place, source in small:
                sp.dma_start(place, source).then_inc(small_landed, 16)
            with turns(sp, n, 8, raw=4) as i:
                for r in range(4):
                    load(sp, n, (whole(), kslab(d["ada_w"][0], r, i * NB), LAND))
                    
            w = d["sgu_w_in"][0]
            sp_pairs(sp, n, w, W2, 4, ada=(d["ada_w"][0], 2 * D))
            ada1 = d["ada_w"][1]
            for c in range(2):
                sp_pairs(sp, n, w, c * D, 2, ada=(ada1, (6 * c) * NB))
                sp_pairs(sp, n, w, 2 * W2 + c * D, 2, ada=(ada1, (6 * c + 2) * NB))
                sp_pairs(sp, n, d["sgu_w_out"][0], 0, 2, k0=4 * c, ada=(ada1, (6 * c + 4) * NB))
            w = d["mla_w_in"][0]
            for g in range(4):
                load(sp, n, (lambda s: whole()(s)[:, :, 0:448], kslab(w, g, 0, 448), LAND))
            for g in range(4):
                load(sp, n, (whole(), kslab(w, g, 448), LAND))
            wk = w.rearrange("(k p) n -> p k n", p=P)
            load(sp, n, (lambda s: whole(16, P)(s)[:, :, 0:64], wk[:, :, 960:1024], 16),
                 (lambda s: whole(16, P)(s)[:, :, 64:96], wk[:, :, 992:1024], 16),
                 (lambda s: whole(16, P)(s)[:, :, 96:128], wk[:, :, 960:992], 32))
            uq = d["mla_w_uq"][0].rearrange("(k p) n -> p k n", p=112)
            ukv = d["mla_w_ukv"][0].rearrange("(k p) n -> p k n", p=P)
            with turns(sp, n, 4, raw=8) as i:
                for j in range(4):
                    q0 = i * (4 * 192) + j * 192
                    load(sp, n,
                         (lambda s: whole()(s)[0:112, :, 0:192], uq[:, :, bass.ds(q0, 192)], 16),
                         (lambda s: whole()(s)[0:112, :, 192:224], uq[:, :, bass.ds(q0 + 160, 32)], 16),
                         (lambda s: whole()(s)[0:112, :, 224:256], uq[:, :, bass.ds(q0 + 128, 32)], 16),
                         (lambda s: whole()(s)[:, :, 256:512], ukv[:, :, bass.ds(i * 1024 + j * 256, 256)], 16))
                    load(sp, n, (whole(), kslab(w, j, i * NB + 1024), LAND))
            sp_pairs(sp, n, d["mla_w_out"][0], 0, 2)
            w = d["w_in_2"][0]
            for b in range(2):
                sp_block(sp, n, w, 4096 + b * NB)
            for g in range(2):
                load(sp, n, (whole(8, 256), kslab(w, g, 5120, 256, 8), LAND))
            wg = w.rearrange("(k p) n -> p k n", p=P)
            for half in range(2):
                with turns(sp, n, 4, raw=8) as i:
                    for g in range(4):
                        c0 = i * P + half * 512
                        load(sp, n, *((lambda s, q=q: whole()(s)[:, :, q * P:(q + 1) * P],
                                       wg[:, 4 * g:4 * g + 4, bass.ds(c0 + q * 1024, P)], 16) for q in range(4)))
                    sp_block(sp, n, w, i * NB + (5376 + half * D))
            for m in ("w_hg_out_2", "w_at_out_2"):
                for b in range(4):
                    sp_block(sp, n, d[m][0], b * NB, slabs=2)
            sp_pairs(sp, n, d["w_out_2"][0], 0, 2)
            for c in range(4):
                sp_pairs(sp, n, d["w_up_2"][0], c * D, 2)
                sp_pairs(sp, n, d["w_down_2"][0], 0, 2, k0=4 * c)
            o = out.rearrange("b (t p) n -> p (b t) n", p=P)
            for b in range(4):
                sp.wait_ge(stage_free, 2 + STAGED - 8 + 2 * (b + 1))
                sp.dma_start(o[:, :, b * NB:(b + 1) * NB], x[:, :, b * NB:(b + 1) * NB]).then_inc(stored, 16)
            sp.wait_ge(stored, 64)

        def hi_next(act, n, ahead=AHEAD):
            q = n.chunk.base + ahead
            r = raw_of(q)
            here = LAND * (r // RAWS + 1)
            if n.raw.turn is not None:
                here = n.raw.turn * (LAND // RAWS * n.raw.each) + here
            act.wait_ge(landed[r % RAWS], here)
            act.wait_ge(chunk_used, n.chunk.at(ahead + 1))
            nc.scalar.activation(hi[:, q % CHUNKS, :], raw[:, r % RAWS, q % 2 * CW:(q % 2 + 1) * CW],
                                 ACT.Copy).then_inc(hi_ready, 1)

        def act_steps(act, n, k, last=False):
            for s in range(k):
                if not last or s < k - AHEAD:
                    hi_next(act, n)
                n.chunk.base += 1

        def act_result(act, n, dst, func=ACT.Copy, aset=None, width=NB):
            act.wait_ge(chunk_used, n.chunk.at(CHUNKS))
            for t in range(T):
                s = n.acc.base // 2 % 2 if aset is None else aset
                if dst is None:
                    act.wait_ge(stage_free, n.stg.at(t + 1))
                to = stage[:, t, :] if dst is None else dst(t)
                nc.scalar.activation(to, ps[:, 2 * s + t, 0:width], func).then_inc(acc_free, 1)
            n.acc.base += 2
            if dst is None:
                n.stg.base += 2

        def mla_out(act, n, i, j):
            act.wait_ge(m_pv, n.head.at(1))
            act.wait_ge(m_rcp, n.head.at())
            for t in range(T):
                nc.scalar.activation(v[:, t, bass.ds(i * NB + (D + j * P), P)], ps[:, 6 + t, 384:512], ACT.Copy,
                                     scale=m_rec[:, t:t + 1]).then_inc(m_out, 1)

        def act_pairs(act, n, n_turns, dst, func=ACT.Copy, raws=8, last=False):
            add = dict(raw=raws, chunk=16, acc=4, stg=0 if dst else 4)
            with turns(act, n, n_turns, **add) as i:
                for b in range(2):
                    act_steps(act, n, 8)
                    act_result(act, n, (lambda t: dst(i, b, t)) if dst else None, func)

        def act_squares(act, n, src):
            for t in range(T):
                one = src(t)
                if n.sq.base or t:
                    act.wait_ge(n_ss, n.sq.base + t)
                nc.scalar.activation(junk[:, 0:one.shape[-1]], one, ACT.Square, accum_out=ss[:, t:t + 1]).then_inc(n_ss, 1)
            n.sq.base += 2

        def act_root(act, n):
            act.wait_ge(n_var, n.nrm.base + 1)
            if n.nrm.base:
                act.wait_ge(n_rstd, n.nrm.base)
            nc.scalar.activation(sd[:, :], var[:, :], ACT.Sqrt).then_inc(n_sd, 1)
            n.nrm.base += 1

        def act_split(act, n, groups, dst, w=P):
            for g in range(groups):
                act.wait_ge(t_kept, n.tg.base + 1)
                if g == 0:
                    act.wait_ge(chunk_used, n.chunk.base + CHUNKS)
                nc.scalar.activation(dst[0:w, 2 * g:2 * g + 2, :],
                                     tf[0:w, n.tg.base % 2, :].rearrange("p (k s) -> p k s", k=2), ACT.Copy).then_inc(t_hi, 1)
                n.tg.base += 1

        @block.scalar
        def _(act):
            n = Counts()
            for t in range(T):
                act.dma_start(x[:, t, :], d["x"][0, t * P:(t + 1) * P, :]).then_inc(x_landed, 16)
            act.dma_start(ws[:, :, :], d["sgu_w_s"][0].rearrange("g t s -> t g s")).then_inc(gain_landed, 16)
            act.wait_ge(vec_kept, 1)
            nc.scalar.activation(cond[:, :], va[:, A_C:A_C + KT], ACT.Silu).then_inc(cond_ready, 1)
            act.wait_ge(x_landed, 32)
            act_squares(act, n, lambda t: x[:, t, :])
            act_root(act, n)
            for k in range(AHEAD):
                hi_next(act, n, k)
            act_split(act, n, 8, a_hi)
            act.dma_start(y[:, :, :].rearrange("p t n -> p (t n)"),
                          d["sgu_norm_g"][0].partition_broadcast(P)).then_inc(gain_landed, 16)
            act_pairs(act, n, 4, lambda i, b, t: v[:, t, bass.ds(i * (2 * NB) + b * NB, NB)], ACT.Gelu, raws=12)
            act_root(act, n)
            for g in range(8):
                act.wait_ge(sp_mixed, 2 * g + 1)
                for e in range(2):
                    gg = 2 * g + e
                    ins = nc.scalar.activation(v[:, 0, gg * S:(gg + 1) * S], ps[:, 4 + g % 2, e * S:(e + 1) * S],
                                               ACT.Identity, bias=vb[:, B_BS + gg:B_BS + gg + 1])
                ins.then_inc(vm_act, 1)
            for c in range(2):
                act_pairs(act, n, 2, None, ACT.Gelu, raws=12)
                act_pairs(act, n, 2, None, ACT.Silu, raws=12)
                act_split(act, n, 8, b_hi)
                act_pairs(act, n, 2, (lambda i, b, t: y[:, t, bass.ds(i * (2 * NB) + b * NB, NB)]) if c == 0 else None, raws=12)
            act.wait_ge(stage_free, 2 + n.stg.base)
            act_squares(act, n, lambda t: y[:, t, :])
            act_root(act, n)
            act.wait_ge(x_updated, 1)
            act_squares(act, n, lambda t: x[:, t, :])
            act_root(act, n)
            act_split(act, n, 8, a_hi)
            act_steps(act, n, 8)
            act_result(act, n, lambda t: v[:, t, D:D + 448], width=448)
            act_steps(act, n, 8)
            act_result(act, n, lambda t: v[:, t, D + 448:D + 960])
            act.wait_ge(acc_free, 4 + n.acc.base)
            act_squares(act, n, lambda t: v[:, t, D:D + 448])
            act_root(act, n)
            act_squares(act, n, lambda t: v[:, t, D + 448:D + 960])
            act_root(act, n)
            act_steps(act, n, 2)
            act_split(act, n, 2, b_hi, 112)
            act_split(act, n, 2, b_hi[:, 4:8, :])
            with turns(act, n, 4, raw=8, chunk=16, acc=2, head=4) as i:
                for j in range(4):
                    act_steps(act, n, 2)
                    act.wait_ge(chunk_used, n.chunk.at(CHUNKS))
                    nc.scalar.activation(m_qn, ps[:, 4, 0:S], ACT.Copy).then_inc(m_evac, 1)
                    nc.scalar.activation(m_kn, ps[:, 5, 0:S], ACT.Copy).then_inc(m_evac, 1)
                    act.wait_ge(m_pv, n.head.at(1))
                    nc.scalar.activation(m_v, ps[:, 5, S:2 * S].rearrange("p (t c) -> p t c", t=T), ACT.Copy).then_inc(m_evac, 1)
                    if j:
                        mla_out(act, n, i, j - 1)
                    act_steps(act, n, 1)
                    act.wait_ge(m_maxed, n.head.at(1))
                    for t in range(T):
                        c0, c1 = (0, P) if t == 0 else (P, 3 * P)
                        nc.scalar.activation(m_s[:, c0:c1], m_s[:, c0:c1], ACT.Exp, bias=m_max[:, t:t + 1],
                                             accum_out=m_sum[:, t:t + 1]).then_inc(m_exped, 1)
                    act_steps(act, n, 1)
                    n.head.base += 1
                mla_out(act, n, i, 3)
                act_result(act, n, lambda t: v[:, t, bass.ds(i * NB, NB)], ACT.Silu, aset=0)
            act_split(act, n, 8, b_hi)
            act_pairs(act, n, 2, lambda i, b, t: y[:, t, bass.ds(i * (2 * NB) + b * NB, NB)])
            act.wait_ge(acc_free, 4 + n.acc.base)
            act_squares(act, n, lambda t: y[:, t, :])
            act_root(act, n)
            act.wait_ge(x_updated, 2)
            act_squares(act, n, lambda t: x[:, t, :])
            act_root(act, n)
            act_split(act, n, 8, a_hi)
            for g in range(2):
                act_steps(act, n, 8)
                act_result(act, n, lambda t: y[:, t, g * NB:(g + 1) * NB])
            act_steps(act, n, 4)
            act_result(act, n, lambda t: y[:, t, 2 * NB:2 * NB + 256], width=256)
            rd = [(rows[:, 0:128], "hg_norm_2"), (rows[:, 128:192], "q_norm_2"), (rows[:, 192:256], "k_norm_2"), (rows[:, 256:272], "sinks_2")]
            for place, name in rd:
                act.dma_start(place, d[name][0].partition_broadcast(P)).then_inc(rows_landed, 16)
            act.dma_start(lb[:, :], d["lb_logits_2"][0].partition_broadcast(P)).then_inc(rows_landed, 16)
            act.wait_ge(lb_diff, 1)
            nc.scalar.activation(oml[:, :], oml[:, :], ACT.Exp).then_inc(lb_exp, 1)
            act.wait_ge(q_ss, 1)
            nc.scalar.activation(nrm[:, 1, :, :], nrm[:, 0, :, :], ACT.Sqrt).then_inc(q_sd, 1)
            for half in range(2):
                with turns(act, n, 4, raw=8, chunk=16, acc=4, swa=2, hg=1) as i:
                    for e in range(2):
                        act_steps(act, n, 2)
                        act.wait_ge(w_maxed, n.swa.at(1))
                        for t in range(T):
                            c0, c1 = (0, P) if t == 0 else (P, 3 * P)
                            nc.scalar.activation(swa_s[:, c0:c1], swa_s[:, c0:c1], ACT.Exp, bias=w_nm[:, t:t + 1],
                                                 accum_out=w_sum[:, t:t + 1]).then_inc(w_exped, 1)
                        nc.scalar.activation(w_es[:, :], w_nm[:, :], ACT.Exp,
                                             bias=rows[:, bass.ds(i * 2 + (256 + 8 * half + e), 1)]).then_inc(w_exped, 1)
                        act_steps(act, n, 2)
                        act.wait_ge(w_pv, n.swa.at(1))
                        act.wait_ge(w_rcp, n.swa.at(1))
                        for t in range(T):
                            nc.scalar.activation(y[:, t, bass.ds(i * P + (1024 + half * 512 + e * 64), 64)],
                                                 ps[:, 6, t * 64:(t + 1) * 64], ACT.Copy, scale=w_rec[:, t:t + 1]).then_inc(w_out, 1)
                        n.swa.base += 1
                    act.wait_ge(chunk_used, n.chunk.at(CHUNKS))
                    s2 = n.acc.base // 2 % 2 * 2
                    part = lambda q: ps[:, s2:s2 + 2, q * P:(q + 1) * P]
                    nc.scalar.activation(h_f[:, :, :], part(1), ACT.Sigmoid).then_inc(h_in, 1)
                    nc.scalar.activation(h_q[:, :, :], part(0), ACT.Silu).then_inc(h_in, 1)
                    act.wait_ge(h_done, n.hg.at(1))
                    nc.scalar.activation(h_gate[:, :, :], part(3), ACT.Silu).then_inc(h_in, 1)
                    nc.scalar.activation(h_v[:, :, :], part(2), ACT.Copy).then_inc(acc_free, 2)
                    n.acc.base += 2
                    act.wait_ge(h_fg, n.hg.at(1))
                    nc.scalar.activation(h_g[:, :, :], h_f[:, :, :], ACT.Ln).then_inc(h_log, 1)
                    act_steps(act, n, 2)
                    act.wait_ge(h_turned, n.hg.at(1))
                    nc.scalar.activation(h_cum[:, :], ps[:, 5, 0:S], ACT.Copy).then_inc(h_cumk, 1)
                    act.wait_ge(h_diff, n.hg.at(1))
                    nc.scalar.activation(h_e[:, 0, :], h_d[:, 0, :], ACT.Exp).then_inc(h_exp, 1)
                    nc.scalar.activation(h_e[:, 1, :], h_d[:, 0, :], ACT.Exp, scale=-1.0).then_inc(h_exp, 1)
                    nc.scalar.activation(h_e[:, 2, :], h_cum[:, :], ACT.Exp).then_inc(h_exp, 1)
                    nc.scalar.activation(h_e[:, 3, :], h_d[:, 1, :], ACT.Exp, scale=-1.0).then_inc(h_exp, 1)
                    act_steps(act, n, 3)
                    act.wait_ge(h_amm, n.hg.at(1))
                    nc.scalar.activation(h_kt[:, :, :], ps[:, 7, 0:S].rearrange("p (t c) -> p t c", t=T), ACT.Copy).then_inc(h_ktk, 1)
                    act_steps(act, n, 2)
                    act.wait_ge(h_om, n.hg.at(1))
                    for t in range(T):
                        nc.scalar.activation(h_junk[:, t, :], ps[:, 5, t * P:(t + 1) * P], ACT.Square,
                                             accum_out=h_n[:, 0, t:t + 1]).then_inc(h_sq, 1)
                    act.wait_ge(h_v1, n.hg.at(1))
                    nc.scalar.activation(h_n[:, 1, :], h_n[:, 0, :], ACT.Sqrt).then_inc(h_sd1, 1)
                    n.hg.base += 1
                    act_steps(act, n, 1)
                    act_result(act, n, lambda t: v[:, t, bass.ds(i * NB + half * D, NB)], ACT.Sigmoid)
            act_split(act, n, 4, b_hi)
            act_split(act, n, 4, b_hi[:, 8:16, :])
            for b in range(8):
                act_steps(act, n, 4)
                act_result(act, n, None)
            act_split(act, n, 8, a_hi)
            act_pairs(act, n, 2, None)
            act.wait_ge(stage_free, 2 + n.stg.base)
            act_squares(act, n, lambda t: x[:, t, :])
            act_root(act, n)
            act_split(act, n, 8, a_hi)
            for c in range(4):
                act_pairs(act, n, 2, None, ACT.Relu)
                act_split(act, n, 8, b_hi)
                if c < 3:
                    act_pairs(act, n, 2, None)
                else:
                    for b in range(4):
                        act_steps(act, n, 8, last=(b == 3))
                        act_result(act, n, None)
            assert n.stg.base == STAGED

        def lo_next(dve, n, ahead=AHEAD):
            q = n.chunk.base + ahead
            r = raw_of(q)
            dve.wait_ge(hi_ready, n.chunk.at(ahead + 1))
            nc.vector.tensor_tensor(lo[:, q % CHUNKS, :], raw[:, r % RAWS, q % 2 * CW:(q % 2 + 1) * CW],
                                    hi[:, q % CHUNKS, :].bitcast(F32), ALU.subtract).then_inc(lo_ready, 1)
            if q % 2:
                raw_done(dve, n)

        def raw_done(dve, n):
            k = n.raw.base % RAWS
            nc.vector.memset(tick[:, k:k + 1], 0.0).then_inc(raw_free, 1)
            n.raw.base += 1

        def then(dve, n, ins):
            ins.then_inc(dv_step, 1)
            n.dv.base += 1
            dve.wait_ge(dv_step, n.dv.at())

        def ada_sum(dve, n, a):
            k = n.raw.base % RAWS
            here = LAND * (n.raw.base // RAWS + 1)
            if n.raw.turn is not None:
                here = n.raw.turn * (LAND // RAWS * n.raw.each) + here
            dve.wait_ge(landed[k], here)
            for j in range(4):
                w, c = raw[:, k, j * NB:(j + 1) * NB], cond[:, 4 * a + j:4 * a + j + 1]
                if a == j == 0:
                    then(dve, n, nc.vector.tensor_scalar(acc[:, :], w, c, None, ALU.mult))
                    continue
                ins = nc.vector.scalar_tensor_tensor(out=acc[:, :], in0=w, scalar=c, in1=acc[:, :], op0=ALU.mult, op1=ALU.add)
                if a == j == 3:
                    ins.then_inc(ada_acc, 1)
                else:
                    then(dve, n, ins)
            raw_done(dve, n)

        def ada_keep(dve, n, layer, col):
            dve.wait_ge(ada_summed, n.ada.at(1))
            nc.vector.tensor_copy(mod[:, layer, bass.ds(col, 4)], ps[:, 7, 0:4]).then_inc(ada_kept, 1)
            n.ada.base += 1

        def dve_steps(dve, n, k, last=False, ada=False):
            for s in range(k):
                if not last or s < k - AHEAD:
                    lo_next(dve, n)
                if ada and n.chunk.base % 4 == 0:
                    ada_sum(dve, n, n.chunk.base // 4 % 4)
                n.chunk.base += 1

        def dve_norm(dve, n, width):
            n.sq.base += 2
            dve.wait_ge(n_ss, n.sq.base)
            nc.vector.tensor_scalar(var[:, :], ss[:, :], 1.0 / width, EPS, ALU.mult, ALU.add).then_inc(n_var, 1)
            dve.wait_ge(n_sd, n.nrm.base + 1)
            nc.vector.reciprocal(rstd[:, :], sd[:, :]).then_inc(n_rstd, 1)
            n.nrm.base += 1
            dve.wait_ge(n_rstd, n.nrm.base)

        def dve_split(dve, n, groups, hi_to, lo_to, w=P, scale=None, shift=None):
            def rest(g):
                dve.wait_ge(t_hi, g + 1)
                k = 2 * (g - first)
                nc.vector.tensor_tensor(lo_to[0:w, k:k + 2, :], tf[0:w, g % 2, :].rearrange("p (k s) -> p k s", k=2),
                                        hi_to[0:w, k:k + 2, :].bitcast(F32), ALU.subtract).then_inc(t_lo, 1)

            first = n.tg.base
            for g in range(first, first + groups):
                dve.wait_ge(t_turned, g + 1)
                if g >= 2:
                    dve.wait_ge(t_lo, g - 1)
                if scale is None:
                    nc.vector.tensor_copy(tf[0:w, g % 2, :], ps[0:w, 4 + g % 2, :]).then_inc(t_kept, 1)
                else:
                    for e in range(2):
                        k = 2 * (g - first) + e
                        to, a = tf[0:w, g % 2, e * S:(e + 1) * S], ps[0:w, 4 + g % 2, e * S:(e + 1) * S]
                        if shift is None:
                            ins = nc.vector.tensor_scalar(to, a, scale(k), None, ALU.mult)
                        else:
                            ins = nc.vector.tensor_scalar(to, a, scale(k), shift(k), ALU.mult, ALU.add)
                    ins.then_inc(t_kept, 1)
                if g > first:
                    rest(g - 1)
            rest(first + groups - 1)
            n.tg.base += groups

        def dve_pairs(dve, n, n_turns, raws=8, stats=None, ada=None):
            add = dict(raw=raws, chunk=16, acc=4, ada=1 if ada else 0, dv=15 if ada else 0)
            with turns(dve, n, n_turns, **add) as i:
                for b in range(2):
                    dve_steps(dve, n, 8, ada=ada is not None)
                    n.acc.base += 2
                    if stats:
                        stats(i, b)
                if ada:
                    ada_keep(dve, n, ada[0], i * 4 + ada[1])

        def norm_x(dve, n):
            dve_norm(dve, n, D)
            for t in range(T):
                nc.vector.tensor_scalar(y[:, t, :], x[:, t, :], rstd[:, t:t + 1], None, ALU.mult).then_inc(n_out, 1)

        def layer_in(dve, n, layer):
            then(dve, n, nc.vector.scalar_tensor_tensor(
                out=hscale[:, :], in0=mod[:, layer, 16:32], scalar=1.0, in1=va[:, A_PRE + 16 * layer:A_PRE + 16 * layer + 16],
                op0=ALU.add, op1=ALU.mult))
            dve_split(dve, n, 8, a_hi, a_lo, scale=lambda k: hscale[:, k:k + 1], shift=lambda k: mod[:, layer, k:k + 1])

        def layer_out(dve, n, layer):
            dve_norm(dve, n, D)
            dve.wait_ge(gate_rows, layer + 1)
            for t in range(T):
                then(dve, n, nc.vector.scalar_tensor_tensor(out=y[:, t, :], in0=y[:, t, :], scalar=rstd[:, t:t + 1],
                     in1=ps[:, 4:8, :].rearrange("p a b -> p (a b)"), op0=ALU.mult, op1=ALU.mult))
            for t in range(T):
                ins = nc.vector.tensor_tensor(x[:, t, :], x[:, t, :], y[:, t, :], ALU.add)
            ins.then_inc(x_updated, 1)

        def gate_cols(dve, n, layer):
            nc.vector.tensor_tensor(gpost[:, :], mod[:, layer, 32:48], va[:, A_POST + 16 * layer:A_POST + 16 * layer + 16],
                                    ALU.mult).then_inc(gain_cols, 1)

        @block.vector
        def _(dve):
            n = Counts()
            dve.wait_ge(vec_turned, 1)
            nc.vector.tensor_copy(va[:, :], ps[:, 4, 0:A_ROWS]).then_inc(vec_kept, 1)
            nc.vector.tensor_copy(vb[:, :], ps[:, 4, P:P + B_ROWS]).then_inc(vec_kept, 1)
            norm_x(dve, n)
            dve.wait_ge(cond_ready, 1)
            with turns(dve, n, 8, raw=4, ada=1, dv=15) as i:
                for a in range(4):
                    ada_sum(dve, n, a)
                ada_keep(dve, n, 0, i * 4)
            dve.wait_ge(ada_kept, 1 + 8)
            then(dve, n, nc.vector.tensor_tensor(mod[:, 0, 0:32], mod[:, 0, 0:32], vb[:, B_ADA:B_ADA + 32], ALU.add))
            for k in range(AHEAD):
                lo_next(dve, n, k)
            layer_in(dve, n, 0)

            def stats(i, b):
                dve.wait_ge(acc_free, n.acc.at(4))
                for t in range(T):
                    nc.vector.bn_stats(cnt[:, t, bass.ds(i * 2 + b, 1), :], v[:, t, bass.ds(i * (2 * NB) + b * NB, NB)])\
                        .then_inc(v_ready, 1)

            dve_pairs(dve, n, 4, 12, stats, ada=(0, 32))
            for g in range(4):
                dve.wait_ge(sp_turned, g + 1)
                bank = ps[:, 4 + g % 2, :].rearrange("p (g t) -> p g t", g=4)
                nc.vector.tensor_copy(wt[:, 4 * g:4 * g + 4, 64:128], bank[:, :, 64:128])
                nc.vector.tensor_copy(wt[0:64, 4 * g:4 * g + 4, 0:64], bank[0:64, :, 0:64]).then_inc(sp_kept, 1)
            dve.wait_ge(v_ready, 16)
            for t in range(T):
                ins = nc.vector.bn_aggr(agg[:, t, :], cnt[:, t, :, :].rearrange("p a b -> p (a b)"))
            then(dve, n, ins)
            nc.vector.tensor_scalar(var[:, :], agg[:, :, 1], 1.0, EPS, ALU.mult, ALU.add).then_inc(n_var, 1)
            dve.wait_ge(n_sd, n.nrm.base + 1)
            nc.vector.reciprocal(rstd[:, :], sd[:, :]).then_inc(n_rstd, 1)
            n.nrm.base += 1
            dve.wait_ge(n_rstd, n.nrm.base)
            dve.wait_ge(gain_landed, 32)
            grow = y[:, :, :].rearrange("p t n -> p (t n)")
            for t in range(T):
                then(dve, n, nc.vector.tensor_scalar(v[:, t, :], v[:, t, :], agg[:, t, 0:1], rstd[:, t:t + 1], ALU.subtract, ALU.mult))
                nc.vector.tensor_tensor(v[:, t, :], v[:, t, :], grow, ALU.mult).then_inc(ln_done, 1)
            for g in range(8):
                dve.wait_ge(sp_mixed, 2 * g + 2)
                for e in range(2):
                    gg = 2 * g + e
                    ins = nc.vector.tensor_scalar(v[:, 1, gg * S:(gg + 1) * S], ps[:, 6 - 3 * (g % 2), e * S:(e + 1) * S],
                                                  vb[:, B_BS + gg:B_BS + gg + 1], None, ALU.add)
                ins.then_inc(vm_vec, 1)
            for c in range(2):
                dve_pairs(dve, n, 2, 12, ada=(1, 24 * c))
                dve_pairs(dve, n, 2, 12, ada=(1, 24 * c + 8))
                dve_split(dve, n, 8, b_hi, b_lo)
                dve_pairs(dve, n, 2, 12, ada=(1, 24 * c + 16))
            dve.wait_ge(ada_kept, 1 + 24)
            nc.vector.tensor_tensor(mod[:, 0, 32:48], mod[:, 0, 32:48], vb[:, B_ADA + 32:B_ADA + 48], ALU.add)
            then(dve, n, nc.vector.tensor_tensor(mod[:, 1, :], mod[:, 1, :], vb[:, B_ADA + 48:B_ADA + 96], ALU.add))
            gate_cols(dve, n, 0)
            layer_out(dve, n, 0)
            norm_x(dve, n)
            layer_in(dve, n, 1)
            dve_steps(dve, n, 8)
            dve_steps(dve, n, 8)
            n.acc.base += 4
            cq = [v[:, t, D:D + 448] for t in range(T)]
            ckv = [v[:, t, D + 448:D + 960] for t in range(T)]
            dve_norm(dve, n, 448)
            for t in range(T):
                nc.vector.tensor_scalar(cq[t], cq[t], rstd[:, t:t + 1], None, ALU.mult).then_inc(c_ready, 1)
            dve_norm(dve, n, 512)
            for t in range(T):
                nc.vector.tensor_scalar(ckv[t], ckv[t], rstd[:, t:t + 1], None, ALU.mult).then_inc(c_ready, 1)
            dve_steps(dve, n, 2)

            def rotate(bank, c0, to, signal):
                nc.vector.tensor_tensor(m_t[0:64], ps[0:64, bank, c0:c0 + S], cst[0:64, C_ROPE:C_ROPE + S], ALU.mult)
                then(dve, n, nc.vector.tensor_tensor(m_t2[0:64], ps[64:128, bank, c0:c0 + S], cst[64:128, C_ROPE:C_ROPE + S], ALU.mult))
                nc.vector.tensor_tensor(to, m_t[0:64], m_t2[0:64], ALU.add).then_inc(signal, 1)

            dve.wait_ge(chunk_used, n.chunk.base + CHUNKS)
            rotate(6, 0, m_kr[0:64], kr_kept)
            dve_split(dve, n, 2, b_hi, b_lo, 112, scale=lambda k: vb[0:112, B_QG + k:B_QG + k + 1])
            dve_split(dve, n, 2, b_hi[:, 4:8, :], b_lo[:, 4:8, :], scale=lambda k: va[:, A_KVG + k:A_KVG + k + 1])
            with turns(dve, n, 4, raw=8, chunk=16, acc=2, head=4, dv=12) as i:
                for j in range(4):
                    dve_steps(dve, n, 2)
                    dve.wait_ge(chunk_used, n.chunk.at(CHUNKS))
                    dve.wait_ge(m_evac, 3 * n.head.at() + 1)
                    rotate(4, S, m_qr[0:64], m_roped)
                    dve_steps(dve, n, 1)
                    dve.wait_ge(m_scored, n.head.at(1))
                    then(dve, n, nc.vector.scalar_tensor_tensor(out=m_s, in0=ps[:, 6, 0:384], scalar=MLA_SCALE,
                         in1=cst[:, C_MASK:C_MASK + 384], op0=ALU.mult, op1=ALU.add))
                    nc.vector.tensor_reduce(m_t[:, 0:1], m_s[:, 0:P], AX, ALU.max)
                    then(dve, n, nc.vector.tensor_reduce(m_t[:, 1:2], m_s[:, P:3 * P], AX, ALU.max))
                    nc.vector.tensor_scalar(m_max, m_t[:, 0:2], -1.0, None, ALU.mult).then_inc(m_maxed, 1)
                    dve_steps(dve, n, 1)
                    dve.wait_ge(m_exped, 2 * n.head.at(1))
                    nc.vector.reciprocal(m_rec, m_sum).then_inc(m_rcp, 1)
                    dve.wait_ge(m_turned, n.head.at(1))
                    nc.vector.tensor_copy(m_pt, ps[:, 7, 0:384]).then_inc(m_ptk, 1)
                    n.head.base += 1
                n.acc.base += 2
            dve_split(dve, n, 8, b_hi, b_lo)
            gate_cols(dve, n, 1)
            dve_pairs(dve, n, 2)
            layer_out(dve, n, 1)
            norm_x(dve, n)
            dve_split(dve, n, 8, a_hi, a_lo, scale=lambda k: va[:, A_MIX + k:A_MIX + k + 1])
            dve_steps(dve, n, 20)
            n.acc.base += 6
            dve.wait_ge(rows_landed, 80)
            nc.vector.tensor_tensor(oml[:, :], lb[:, :], lb[:, :], ALU.subtract).then_inc(lb_diff, 1)
            dve.wait_ge(lb_exp, 1)
            then(dve, n, nc.vector.reciprocal(lb[:, :], oml[:, :]))
            then(dve, n, nc.vector.tensor_tensor(oml[:, :], oml[:, :], lb[:, :], ALU.mult))
            then(dve, n, nc.vector.tensor_tensor(lb[:, :], oml[:, :], oml[:, :], ALU.subtract))
            nc.vector.tensor_scalar(oml[:, :], lb[:, :], -1.0, 1.0, ALU.mult, ALU.add).then_inc(lb_ready, 1)
            dve.wait_ge(acc_free, n.acc.base + 4)
            then(dve, n, nc.vector.tensor_tensor(v[:, :, 0:1152], y[:, :, 0:1152], y[:, :, 0:1152], ALU.mult))
            for t in range(T):
                ins = nc.vector.tensor_reduce(nrm[:, 0, t, :], v[:, t, 0:1152].rearrange("p (h c) -> p h c", c=64), AX, ALU.add)
            then(dve, n, ins)
            nc.vector.tensor_scalar(nrm[:, 0, :, :], nrm[:, 0, :, :], 1.0 / 64, EPS, ALU.mult, ALU.add).then_inc(q_ss, 1)
            then(dve, n, nc.vector.tensor_scalar(rows[:, 128:192], rows[:, 128:192], 0.125, None, ALU.mult))
            dve.wait_ge(q_sd, 1)
            then(dve, n, nc.vector.reciprocal(nrm[:, 2, :, :], nrm[:, 1, :, :]))
            for t in range(T):
                yh = y[:, t, 0:1152].rearrange("p (h c) -> p h c", c=64)
                then(dve, n, nc.vector.tensor_tensor(yh, yh, nrm[:, 2, t, :].unsqueeze(2).broadcast_to([P, 18, 64]), ALU.mult))
                nc.vector.tensor_tensor(yh[:, 0:16, :], yh[:, 0:16, :], rows[:, 128:192].unsqueeze(1).broadcast_to([P, 16, 64]), ALU.mult).then_inc(q_normed, 1)
                for e in range(2):
                    ins = nc.vector.tensor_tensor(kdup[:, t, :, e * 64:(e + 1) * 64], yh[:, 16:18, :],
                                                  rows[:, 192:256].unsqueeze(1).broadcast_to([P, 2, 64]), ALU.mult)
                    ins.then_inc(q_normed, 1)
                nc.vector.tensor_copy(v_at[:, t, :], y[:, t, 1152:1280]).then_inc(q_normed, 1)
            for g in range(5):
                dve.wait_ge(q_turned, g + 1)
                to = qt_all[:, 2 * g:2 * g + 2, :] if g < 4 else kt_all[:, :, :]
                nc.vector.tensor_copy(to, ps[:, 4 + g % 2, :].rearrange("p (k s) -> p k s", k=2)).then_inc(q_kept, 1)
            for half in range(2):
                with turns(dve, n, 4, raw=8, chunk=16, acc=4, swa=2, hg=1, dv=9) as i:
                    for e in range(2):
                        dve_steps(dve, n, 1)
                        slope = cst[:, bass.ds(i * 2 + (C_SLOPE + 8 * half + e), 1)]
                        sink = rows[:, bass.ds(i * 2 + (256 + 8 * half + e), 1)]
                        dve.wait_ge(w_scored, n.swa.at(2))
                        then(dve, n, nc.vector.scalar_tensor_tensor(out=swa_s[:, :], in0=cst[:, C_DIST:C_DIST + 384], scalar=slope,
                             in1=ps[:, 4, 0:384], op0=ALU.mult, op1=ALU.add))
                        nc.vector.tensor_reduce(w_rec[:, 0:1], swa_s[:, 0:P], AX, ALU.max)
                        then(dve, n, nc.vector.tensor_reduce(w_rec[:, 1:2], swa_s[:, P:3 * P], AX, ALU.max))
                        nc.vector.tensor_scalar(w_nm[:, :], w_rec[:, :], sink, -1.0, ALU.max, ALU.mult).then_inc(w_maxed, 1)
                        dve_steps(dve, n, 2)
                        dve.wait_ge(w_exped, 3 * n.swa.at(1))
                        then(dve, n, nc.vector.tensor_tensor(w_sum[:, :], w_sum[:, :], w_es[:, :], ALU.add))
                        nc.vector.reciprocal(w_rec[:, :], w_sum[:, :]).then_inc(w_rcp, 1)
                        dve.wait_ge(w_turned, n.swa.at(1))
                        nc.vector.tensor_copy(swa_pt[:, :], ps[:, 5, 0:384]).then_inc(w_ptk, 1)
                        dve_steps(dve, n, 1)
                        n.swa.base += 1
                    n.acc.base += 2
                    dve_steps(dve, n, 2)
                    dve.wait_ge(h_cumk, n.hg.at(1))
                    cum = h_cum[:, :].rearrange("p (c s) -> p c s", s=64)
                    for k, at in ((0, 31), (1, 63)):
                        ins = nc.vector.tensor_tensor(h_d[:, k, :].rearrange("p (c s) -> p c s", s=64), cum,
                                                      cum[:, :, at:at + 1].broadcast_to([P, 4, 64]), ALU.subtract)
                    ins.then_inc(h_diff, 1)
                    dve.wait_ge(h_exp, 4 * n.hg.at(1))
                    qt, kt = ps[:, 4, 0:S], ps[:, 4, S:2 * S]
                    nc.vector.tensor_tensor(h_e[:, 0, :], h_e[:, 0, :], qt, ALU.mult)
                    nc.vector.tensor_tensor(h_e[:, 1, :], h_e[:, 1, :], kt, ALU.mult)
                    nc.vector.tensor_tensor(h_cum[:, :], h_e[:, 2, :], qt, ALU.mult)
                    nc.vector.tensor_tensor(h_e[:, 3, :], h_e[:, 3, :], kt, ALU.mult).then_inc(h_prod, 1)
                    dve_steps(dve, n, 3)
                    dve.wait_ge(h_amm, n.hg.at(1))
                    nc.vector.memset(tick[:, RAWS:RAWS + 1], 0.0)
                    for t in range(T):
                        ins = nc.vector.copy_predicated(h_a[:, t, :], tri.bitcast(U32), ps[:, 6, t * P:(t + 1) * P])
                    ins.then_inc(h_am, 1)
                    dve.wait_ge(h_upd, n.hg.at(1))
                    then(dve, n, nc.vector.tensor_copy(h_s[:, 0, :], ps[:, 7, 256:384]))
                    then(dve, n, nc.vector.scalar_tensor_tensor(out=h_s[:, 1, :], in0=h_s[:, 0, :], scalar=h_e[:, 2, 127:128],
                         in1=ps[:, 6, 256:384], op0=ALU.mult, op1=ALU.add))
                    nc.vector.scalar_tensor_tensor(out=h_s[:, 2, :], in0=h_s[:, 1, :], scalar=h_e[:, 2, 191:192],
                                                   in1=ps[:, 7, 384:512], op0=ALU.mult, op1=ALU.add).then_inc(h_st, 1)
                    dve_steps(dve, n, 2)
                    dve.wait_ge(h_sq, 2 * n.hg.at(1))
                    nc.vector.tensor_scalar(h_n[:, 0, :], h_n[:, 0, :], 1.0 / P, EPS, ALU.mult, ALU.add).then_inc(h_v1, 1)
                    dve.wait_ge(h_sd1, n.hg.at(1))
                    then(dve, n, nc.vector.reciprocal(h_n[:, 2, :], h_n[:, 1, :]))
                    dve.wait_ge(h_gn, n.hg.at(1))
                    for t in range(T):
                        ins = nc.vector.scalar_tensor_tensor(out=y[:, t, bass.ds(i * P + half * 512, P)], in0=ps[:, 5, t * P:(t + 1) * P],
                                                             scalar=h_n[:, 2, t:t + 1], in1=h_gate[:, t, :], op0=ALU.mult, op1=ALU.mult)
                    ins.then_inc(h_done, 1)
                    n.hg.base += 1
                    dve_steps(dve, n, 1)
                    n.acc.base += 2
            dve_split(dve, n, 4, b_hi, b_lo)
            dve_split(dve, n, 4, b_hi[:, 8:16, :], b_lo[:, 8:16, :])
            dve_steps(dve, n, 32)
            dve_split(dve, n, 8, a_hi, a_lo)
            dve_pairs(dve, n, 2)
            norm_x(dve, n)
            dve_split(dve, n, 8, a_hi, a_lo, scale=lambda k: va[:, A_FFN + k:A_FFN + k + 1])
            for c in range(4):
                dve_pairs(dve, n, 2)
                dve_split(dve, n, 8, b_hi, b_lo)
                if c < 3:
                    dve_pairs(dve, n, 2)
                else:
                    dve_steps(dve, n, 32, last=True)

        def pool_take(pool, n, op):
            for t in range(T):
                pool.wait_ge(acc_free, n.acc.at(5 + t))
                pool.wait_ge(stage_free, n.stg.at(2))
                op(t).then_inc(stage_free, 1)
                n.stg.base += 1
            n.acc.base += 2

        def pool_pairs(pool, n, n_turns, op):
            with turns(pool, n, n_turns, acc=4, stg=4) as i:
                for b in range(2):
                    pool_take(pool, n, lambda t: op(t, lambda base: bass.ds(i * (2 * NB) + (base + b * NB), NB)))

        def tt(out_, a, b, op):
            return nc.gpsimd.tensor_tensor(out_, a, b, op)

        @block.gpsimd
        def _(pool):
            n = Counts()
            pool.sem_inc(raw_free, RAWS)
            pool.sem_inc(chunk_used, CHUNKS)
            pool.sem_inc(acc_free, 4)
            pool.sem_inc(stage_free, 2)
            for first in (ada_kept, m_pv, h_done, w_scored):
                pool.sem_inc(first, 1)
            pool.sem_inc(m_out, 2)
            pool.sem_inc(w_out, 2)
            nc.gpsimd.memset(tf[:, :, :], 0.0).then_inc(set_up, 1)
            nc.gpsimd.memset(ones[:, :], 1.0).then_inc(set_up, 1)
            pool.wait_ge(set_up, 2)
            nc.gpsimd.memset(wt[64:128, :, 0:64], 0.0).then_inc(wt_zero, 1)
            n.acc.base = 16
            pool.wait_ge(vm_vec, 8)
            for c in range(2):
                for _ in range(2):
                    pool_pairs(pool, n, 2, lambda t, at: tt(v[:, t, at(c * D)], v[:, t, at(c * D)], stage[:, t, :], ALU.mult))
                if c == 0:
                    n.acc.base += 8
                else:
                    pool_pairs(pool, n, 2, lambda t, at: tt(y[:, t, at(0)], y[:, t, at(0)], stage[:, t, :], ALU.add))
            n.acc.base += 4
            with turns(pool, n, 4, acc=2) as i:
                pool.wait_ge(acc_free, n.acc.at(6))
                for t in range(T):
                    o = v[:, t, bass.ds(i * NB + D, NB)]
                    tt(o, o, v[:, t, bass.ds(i * NB, NB)], ALU.mult).then_inc(y_ready, 1)
                n.acc.base += 2
            n.acc.base += 8 + 6
            pool.wait_ge(q_turned, 5)
            nc.gpsimd.memset(h_a[:, :, :], 0.0).then_inc(h_a_zero, 1)
            pool.wait_ge(q_kept, 5)
            pool.wait_ge(lb_ready, 1)
            for half in range(2):
                with turns(pool, n, 4, swa=2, hg=1, po=1, acc=4) as i:
                    pool.wait_ge(w_scored, n.swa.at(1))
                    nc.gpsimd.tensor_copy(qt_cur[:, :], qt_all[:, bass.ds(i + 4 * half, 1), :].rearrange("p a s -> p (a s)")).then_inc(q_cur, 1)
                    n.swa.base += 2
                    cols = bass.ds(i * P + half * 512, P)
                    wide = lambda a: a.unsqueeze(1).broadcast_to([P, T, P])
                    pool.wait_ge(h_in, 3 * n.hg.at() + 1)
                    tt(h_f[:, :, :], h_f[:, :, :], wide(oml[:, cols]), ALU.mult).then_inc(po_step, 1)
                    n.po.base += 1
                    pool.wait_ge(po_step, n.po.at())
                    tt(h_f[:, :, :], h_f[:, :, :], wide(lb[:, cols]), ALU.add).then_inc(h_fg, 1)
                    pool.wait_ge(h_fg, n.hg.at(1))
                    tt(h_k[:, :, :], ones[:, :].unsqueeze(1).broadcast_to([P, T, P]), h_f[:, :, :], ALU.subtract).then_inc(h_kf, 1)
                    pool.wait_ge(h_in, 3 * n.hg.at() + 3)
                    tt(h_gate[:, :, :], h_gate[:, :, :], wide(rows[:, 0:P]), ALU.mult).then_inc(h_gn, 1)
                    n.hg.base += 1
                    n.acc.base += 4
            for b in range(4):
                c = slice(b * NB, (b + 1) * NB)
                pool_take(pool, n, lambda t: tt(v[:, t, c], v[:, t, c], stage[:, t, :], ALU.mult))
            for b in range(4):
                c, e = slice(b * NB, (b + 1) * NB), slice(D + b * NB, D + (b + 1) * NB)
                pool_take(pool, n, lambda t: tt(v[:, t, e], v[:, t, e], stage[:, t, :], ALU.mult))
                pool.wait_ge(stage_free, n.stg.at(2))
                for t in range(T):
                    tt(v[:, t, c], v[:, t, c], v[:, t, e], ALU.add).then_inc(y_ready, 1)
            add_x = lambda t, at: tt(x[:, t, at(0)], x[:, t, at(0)], stage[:, t, :], ALU.add)
            pool_pairs(pool, n, 2, add_x)
            for c in range(4):
                pool_pairs(pool, n, 2, lambda t, at: tt(v[:, t, at(c % 2 * D)], stage[:, t, :], stage[:, t, :], ALU.mult))
                pool_pairs(pool, n, 2, add_x)

        def three(out_, x_hi, x_lo, w_hi, w_lo, start, stop, weights_first=False):
            mm = nc.tensor.matmul
            if weights_first:
                mm(out_, w_hi, x_hi, start=start, stop=False)
                mm(out_, w_hi, x_lo, start=False, stop=False)
                return mm(out_, w_lo, x_hi, start=False, stop=stop)
            mm(out_, x_hi, w_hi, start=start, stop=False)
            mm(out_, x_hi, w_lo, start=False, stop=False)
            return mm(out_, x_lo, w_hi, start=False, stop=stop)

        def pe_chunk(pe, n, x2, s, k0, kts, width, first, last):
            pe.wait_ge(lo_ready, n.chunk.at(1))
            c = n.chunk.base % CHUNKS
            for t in range(T):
                for j in range(kts):
                    w = slice(j * (CW // kts), j * (CW // kts) + width)
                    ins = three(ps[:, 2 * s + t, 0:width], x2[0][:, k0 + j, t * P:(t + 1) * P], x2[1][:, k0 + j, t * P:(t + 1) * P],
                                hi[:, c, w], lo[:, c, w], first and j == 0, last and j == kts - 1)
            ins.then_inc(chunk_used, 1)
            n.chunk.base += 1

        def pe_block(pe, n, x2, kts=KT, k0=0, step=2, width=NB, extra=None):
            pe.wait_ge(acc_free, n.acc.at(2))
            s = n.acc.base // 2 % 2
            for c in range(kts // step):
                pe_chunk(pe, n, x2, s, k0 + c * step, step, width, c == 0, (c + 1) * step == kts)
                if extra and c in extra:
                    extra[c]()
            n.acc.base += 2

        def pe_ada(pe, n):
            pe.wait_ge(ada_acc, n.ada.at(1))
            pe.wait_ge(ada_kept, n.ada.at(1))
            for q in range(4):
                ins = nc.tensor.matmul(ps[:, 7, q:q + 1], acc[:, q * P:(q + 1) * P], ones[:, :], start=True, stop=True)
            ins.then_inc(ada_summed, 1)
            n.ada.base += 1

        def pe_pairs(pe, n, x2, n_turns, ada=False):
            with turns(pe, n, n_turns, chunk=16, acc=4, ada=int(ada)):
                pe_block(pe, n, x2)
                pe_block(pe, n, x2, extra={6: lambda: pe_ada(pe, n)} if ada else None)

        def pe_turn(pe, n, groups, src, w=P):
            for g in range(groups):
                if n.tg.base >= 2:
                    pe.wait_ge(t_kept, n.tg.base - 1)
                for e in range(2):
                    for t in range(T):
                        a = src(t, 2 * g + e)
                        ins = nc.tensor.transpose(ps[0:w, 4 + n.tg.base % 2, e * S + t * P:e * S + (t + 1) * P], a, ident)
                ins.then_inc(t_turned, 1)
                n.tg.base += 1
            pe.wait_ge(t_lo, n.tg.base)

        def pe_gate_rows(pe, layer):
            pe.wait_ge(gain_cols, layer + 1)
            for k in range(KT):
                ins = nc.tensor.matmul(ps[:, 4 + k // 4, k % 4 * P:(k % 4 + 1) * P], gpost[:, k:k + 1].broadcast_to([P, P]), ident,
                                       start=True, stop=True)
            ins.then_inc(gate_rows, 1)

        def cols(buf, k0=0):
            return lambda t, k: buf[:, t, k0 + k * P:k0 + (k + 1) * P]

        @block.tensor
        def _(pe):
            n = Counts()
            mm = nc.tensor.matmul
            A, B = (a_hi, a_lo), (b_hi, b_lo)
            pe.wait_ge(small_landed, 160)
            nc.tensor.transpose(ps[:, 4, 0:A_ROWS], tf[0:A_ROWS, 0, 0:P], cst[0:A_ROWS, C_ID:C_ID + A_ROWS])
            nc.tensor.transpose(ps[:, 4, P:P + B_ROWS], tf[0:B_ROWS, 0, P:2 * P], cst[0:B_ROWS, C_ID:C_ID + B_ROWS]).then_inc(vec_turned, 1)
            with turns(pe, n, 8, ada=1):
                pe_ada(pe, n)
            pe.wait_ge(vec_kept, 2)
            pe.wait_ge(n_out, 2)
            pe_turn(pe, n, 8, cols(y))
            pe_pairs(pe, n, A, 4, ada=True)
            pe.wait_ge(gain_landed, 32)
            for g in range(4):
                if g >= 2:
                    pe.wait_ge(sp_kept, g - 1)
                for e in range(4):
                    ins = nc.tensor.transpose(ps[:, 4 + g % 2, e * P:(e + 1) * P], ws[:, 4 * g + e, :], ident)
                ins.then_inc(sp_turned, 1)
            pe.wait_ge(sp_kept, 4)
            pe.wait_ge(wt_zero, 1)
            for g in range(8):
                for t in range(T):
                    pe.wait_ge(ln_done, t + 1)
                    if g >= 2:
                        pe.wait_ge((vm_act, vm_vec)[t], g - 1)
                    bank = 4 + g % 2 if t == 0 else 6 - 3 * (g % 2)
                    for e in range(2):
                        k = 2 * g + e
                        ins = mm(ps[:, bank, e * S:(e + 1) * S], wt[:, k, :], v[:, t, k * S:(k + 1) * S], start=True, stop=True)
                    ins.then_inc(sp_mixed, 1)
            pe.wait_ge(vm_vec, 8)
            for c in range(2):
                pe_pairs(pe, n, A, 2, ada=True)
                pe_pairs(pe, n, A, 2, ada=True)
                n.stg.base += 16
                pe.wait_ge(stage_free, 2 + n.stg.base)
                pe_turn(pe, n, 8, cols(v, c * D))
                pe_pairs(pe, n, B, 2, ada=True)
            pe_gate_rows(pe, 0)
            pe.wait_ge(n_out, 4)
            pe_turn(pe, n, 8, cols(y))
            pe_block(pe, n, A, width=448)
            pe_block(pe, n, A)
            for c in range(2):
                pe.wait_ge(lo_ready, n.chunk.at(1))
                k = n.chunk.base % CHUNKS
                for j in range(8):
                    w = slice(j * P, (j + 1) * P)
                    ins = three(ps[:, 6, 0:S], a_hi[:, 8 * c + j, :], a_lo[:, 8 * c + j, :], hi[:, k, w], lo[:, k, w],
                                c == j == 0, c == 1 and j == 7, True)
                ins.then_inc(chunk_used, 1)
                n.chunk.base += 1
            pe.wait_ge(c_ready, 4)
            pe_turn(pe, n, 2, lambda t, k: v[:, t, D + 112 * k:D + 112 * (k + 1)], 112)
            pe_turn(pe, n, 2, cols(v, D + 448))
            pe.wait_ge(kr_kept, 1)
            with turns(pe, n, 4, chunk=16, acc=2, head=4):
                def values():
                    pe.wait_ge(m_ptk, n.head.at())
                    mm(ps[:, 6, 384:512], m_pt[:, 0:P], m_v[:, 0, :], start=True, stop=True)
                    mm(ps[:, 7, 384:512], m_pt[:, P:2 * P], m_v[:, 0, :], start=True, stop=False)
                    mm(ps[:, 7, 384:512], m_pt[:, 2 * P:3 * P], m_v[:, 1, :], start=False, stop=True).then_inc(m_pv, 1)

                for j in range(4):
                    pe.wait_ge(lo_ready, n.chunk.at(2))
                    c = n.chunk.base
                    part = lambda b, k, q0, q1, rows_=P: b[0:rows_, (c + k // 2) % CHUNKS, k % 2 * NB + q0:k % 2 * NB + q1]
                    for q, o in ((0, ps[:, 4, 0:S]), (P, ps[:, 4, S:2 * S])):
                        for k in range(4):
                            three(o, b_hi[0:112, k, :], b_lo[0:112, k, :], part(hi, k, q, q + P, 112), part(lo, k, q, q + P, 112),
                                  k == 0, k == 3, True)
                    for k in range(4):
                        three(ps[:, 5, 0:S], b_hi[:, 4 + k, :], b_lo[:, 4 + k, :], part(hi, k, 256, 384), part(lo, k, 256, 384),
                              k == 0, k == 3, True)
                    for t in range(T):
                        for k in range(4):
                            ins = three(ps[:, 5, S + t * P:S + (t + 1) * P], b_hi[:, 4 + k, t * P:(t + 1) * P], b_lo[:, 4 + k, t * P:(t + 1) * P],
                                        part(hi, k, 384, 512), part(lo, k, 384, 512), k == 0, k == 3)
                    ins.then_inc(chunk_used, 2)
                    n.chunk.base += 2
                    if j:
                        values()
                    else:
                        pe.wait_ge(acc_free, n.acc.at(4))
                    pe_chunk(pe, n, A, 0, 4 * j, 2, NB, j == 0, False)
                    pe.wait_ge(m_evac, 3 * n.head.at(1))
                    pe.wait_ge(m_roped, n.head.at(1))
                    pe.wait_ge(m_out, 2 * n.head.at(1))
                    for o, q, k1 in ((ps[:, 6, 0:P], slice(0, P), P), (ps[:, 6, P:3 * P], slice(P, S), S)):
                        mm(o, m_qn[:, q], m_kn[:, 0:k1], start=True, stop=False)
                        ins = mm(o, m_qr[0:64, q], m_kr[0:64, 0:k1], start=False, stop=True)
                    ins.then_inc(m_scored, 1)
                    pe_chunk(pe, n, A, 0, 4 * j + 2, 2, NB, False, j == 3)
                    n.head.base += 1
                    pe.wait_ge(m_exped, 2 * n.head.at())
                    for k in range(3):
                        ins = nc.tensor.transpose(ps[:, 7, k * P:(k + 1) * P], m_s[:, k * P:(k + 1) * P], ident)
                    ins.then_inc(m_turned, 1)
                values()
                n.acc.base += 2
            pe.wait_ge(y_ready, 8)
            pe_turn(pe, n, 8, cols(v, D))
            pe_pairs(pe, n, B, 2)
            pe_gate_rows(pe, 1)
            pe.wait_ge(n_out, 6)
            pe_turn(pe, n, 8, cols(y))
            pe_block(pe, n, A)
            pe_block(pe, n, A)
            pe_block(pe, n, A, step=4, width=256)
            pe.wait_ge(q_normed, 8)
            for g in range(5):
                if g >= 2:
                    pe.wait_ge(q_kept, g - 1)
                for e in range(2):
                    for t in range(T):
                        a = y[:, t, (2 * g + e) * P:(2 * g + e + 1) * P] if g < 4 else kdup[:, t, e, :]
                        ins = nc.tensor.transpose(ps[:, 4 + g % 2, e * S + t * P:e * S + (t + 1) * P], a, ident)
                ins.then_inc(q_turned, 1)
            pe.wait_ge(q_kept, 5)
            pe.wait_ge(h_a_zero, 1)
            for half in range(2):
                with turns(pe, n, 4, chunk=16, acc=4, swa=2, hg=1):
                    def w_scores(e):
                        if e == 0:
                            pe.wait_ge(q_cur, n.hg.at(1))
                        r = slice(64 * e, 64 * e + 64)
                        mm(ps[:, 4, 0:P], qt_cur[r, 0:P], kt_all[r, half, 0:P], start=True, stop=True)
                        mm(ps[:, 4, P:3 * P], qt_cur[r, P:S], kt_all[r, half, :], start=True, stop=True).then_inc(w_scored, 1)

                    def w_turn():
                        pe.wait_ge(w_exped, 3 * n.swa.at(1))
                        for k in range(3):
                            ins = nc.tensor.transpose(ps[:, 5, k * P:(k + 1) * P], swa_s[:, k * P:(k + 1) * P], ident)
                        ins.then_inc(w_turned, 1)

                    def w_values():
                        pe.wait_ge(w_ptk, n.swa.at(1))
                        pe.wait_ge(w_out, 2 * n.swa.at(1))
                        vv = [v_at[:, t, 64 * half:64 * half + 64] for t in range(T)]
                        mm(ps[:, 6, 0:64], swa_pt[:, 0:P], vv[0], start=True, stop=True)
                        mm(ps[:, 6, 64:128], swa_pt[:, P:2 * P], vv[0], start=True, stop=False)
                        mm(ps[:, 6, 64:128], swa_pt[:, 2 * P:3 * P], vv[1], start=False, stop=True).then_inc(w_pv, 1)
                        n.swa.base += 1

                    pe_block(pe, n, A, extra={0: lambda: w_scores(0), 2: w_turn, 3: lambda: (w_values(), w_scores(1)),
                                              5: w_turn, 6: w_values})

                    def h_turns():
                        pe.wait_ge(h_kf, n.hg.at(1))
                        pe.wait_ge(h_log, n.hg.at(1))
                        pe.wait_ge(w_out, 2 * n.swa.at(1))
                        for a, c0 in ((h_q, 0), (h_k, S)):
                            for t in range(T):
                                nc.tensor.transpose(ps[:, 4, c0 + t * P:c0 + (t + 1) * P], a[:, t, :], ident)
                        for t in range(T):
                            ins = mm(ps[:, 5, t * P:(t + 1) * P], h_g[:, t, :], tri, start=True, stop=True)
                        ins.then_inc(h_turned, 1)

                    def h_pairs():
                        pe.wait_ge(h_prod, n.hg.at(1))
                        for t in range(T):
                            q = slice(t * P, (t + 1) * P)
                            mm(ps[:, 6, q], h_e[:, 1, q], h_e[:, 0, q], start=True, stop=True)
                        for t in range(T):
                            ins = nc.tensor.transpose(ps[:, 7, t * P:(t + 1) * P], h_e[:, 3, t * P:(t + 1) * P], ident)
                        ins.then_inc(h_amm, 1)

                    def h_states():
                        pe.wait_ge(h_ktk, n.hg.at(1))
                        pe.wait_ge(h_am, n.hg.at(1))
                        for o, t, j in ((ps[:, 7, 256:384], 0, 0), (ps[:, 6, 256:384], 0, 1), (ps[:, 7, 384:512], 1, 0)):
                            r = slice(64 * j, 64 * j + 64)
                            ins = mm(o, h_kt[r, t, :], h_v[r, t, :], start=True, stop=True)
                        ins.then_inc(h_upd, 1)

                    def h_outputs():
                        pe.wait_ge(h_st, n.hg.at(1))
                        for t in range(T):
                            for j in range(2):
                                c = 2 * t + j
                                o = ps[64 * j:64 * j + 64, 5, t * P:(t + 1) * P]
                                mm(o, h_a[:, t, 64 * j:64 * j + 64], h_v[:, t, :], start=True, stop=(c == 0))
                                if c:
                                    ins = mm(o, h_cum[:, 64 * c:64 * c + 64], h_s[:, c - 1, :], start=False, stop=True)
                        ins.then_inc(h_om, 1)

                    pe_block(pe, n, A, extra={1: h_turns, 3: h_pairs, 4: h_states, 5: h_outputs})
                    n.hg.base += 1
            pe.wait_ge(h_done, 1 + 8)
            pe.wait_ge(w_out, 2 + 32)
            pe_turn(pe, n, 4, cols(y))
            pe_turn(pe, n, 4, cols(y, 1024))
            for b in range(8):
                pe_block(pe, n, B, kts=8, k0=8 * (b // 4))
            pe.wait_ge(y_ready, 16)
            pe_turn(pe, n, 8, cols(v))
            pe_pairs(pe, n, A, 2)
            pe.wait_ge(n_out, 8)
            pe_turn(pe, n, 8, cols(y))
            for c in range(4):
                pe_pairs(pe, n, A, 2)
                n.stg.base = 32 + 8 + 16 + 8 + 16 * c + 8
                pe.wait_ge(stage_free, 2 + n.stg.base)
                pe_turn(pe, n, 8, cols(v, c % 2 * D))
                pe_pairs(pe, n, B, 2)


INPUTS = ["x", "c", "ada_w", "ada_b", "pre_g", "post_g", "sgu_w_in", "sgu_norm_g", "sgu_w_s", "sgu_b_s", "sgu_w_out",
          "mla_w_in", "mla_q_norm_g", "mla_kv_norm_g", "mla_w_uq", "mla_w_ukv", "mla_w_out", "norm_mix_2", "w_in_2",
          "lb_logits_2", "hg_norm_2", "q_norm_2", "k_norm_2", "sinks_2", "w_hg_out_2", "w_at_out_2", "w_out_2",
          "norm_ffn_2", "w_up_2", "w_down_2"]


def kernel(**inputs):
    import concourse.bacc as bacc
    from concourse.bass_utils import run_bass_kernel_spmd as run

    nc = bacc.Bacc("TRN2", target_bir_lowering=False, num_devices=1, dynamic_dma_scratch_size=1024)
    arrays, d = {}, {}
    for name in INPUTS:
        arrays[f"in_{name}"] = np.ascontiguousarray(inputs[name])
    arrays["in_constants"] = constants()
    for name, a in arrays.items():
        d[name[3:]] = nc.dram_tensor(name, a.shape, mybir.dt.from_np(a.dtype), kind="ExternalInput").ap()
    out = nc.dram_tensor("out", (1, S, D), F32, kind="ExternalOutput").ap()
    build(nc, d, out)
    result = run(nc, [arrays], core_ids=[0])
    return result.results[0]["out"]
```
